# Optimizing a Trainium2 kernel written in Bass

```python
import math
import jax, jax.numpy as jnp
from jax import lax
import numpy as np

D_MODEL = 1024
BATCH = 1
SEQ = 256
DEPTH = 2

N_MIXERS = 4
MIXER_WIDTH = D_MODEL // N_MIXERS
D_MIX = N_MIXERS * MIXER_WIDTH
GROUPS_PER_MIXER = 4
GROUP_DIM = MIXER_WIDTH // GROUPS_PER_MIXER
D_IN_PROJ = 8 * MIXER_WIDTH
SCONV_K = 3
SGU_CHUNK = 128
CCONV_K = 31
POOL_WINDOWS = (2, 4, 8, 16)
N_XATTN_HEADS = 4
XATTN_HEAD_DIM = D_MODEL // N_XATTN_HEADS
N_MEM = 256
D_FF = 2816
EPS = 1e-6

kernel_name = "hybrid_parallel_group_macaron_decoder"

def rmsnorm(x, g):
    xf = x.astype(jnp.float32)
    y = xf * lax.rsqrt(jnp.mean(xf * xf, axis=-1, keepdims=True) + EPS)
    return (y * g.astype(jnp.float32)).astype(x.dtype)

def layernorm(x, g, b=None):
    xf = x.astype(jnp.float32)
    mu = jnp.mean(xf, axis=-1, keepdims=True)
    var = jnp.mean(jnp.square(xf - mu), axis=-1, keepdims=True)
    y = (xf - mu) * lax.rsqrt(var + EPS) * g.astype(jnp.float32)
    if b is not None:
        y = y + b.astype(jnp.float32)
    return y.astype(x.dtype)

def swiglu_ffn(h, w_in, w_out):
    g, u = jnp.split(h @ w_in, 2, axis=-1)
    return (jax.nn.silu(g) * u) @ w_out

def causal_depthwise_conv(x, w):
    k = w.shape[0]
    return lax.conv_general_dilated(
        x, w[:, None, :].astype(x.dtype), window_strides=(1,), padding=((k - 1, 0),),
        dimension_numbers=("NWC", "WIO", "NWC"), feature_group_count=x.shape[-1])

def mixer_short_conv(bg, cg, xt, conv_w):
    return bg * causal_depthwise_conv(cg * xt, conv_w)

def mixer_spatial_gating(u, v, norm_g, w_s, b_s):
    bsz, s, _ = v.shape
    vn = layernorm(v, norm_g)
    vr = vn.reshape(bsz, s // SGU_CHUNK, SGU_CHUNK, GROUPS_PER_MIXER, GROUP_DIM)
    w_causal = jnp.tril(w_s)
    mixed = jnp.einsum("hts,bcshd->bcthd", w_causal.astype(vr.dtype), vr)
    mixed = mixed + b_s.T[None, None, :, :, None].astype(vr.dtype)
    return u * mixed.reshape(bsz, s, MIXER_WIDTH)

def mixer_conformer_conv(a, g, conv_w, ln_g, ln_b):
    y = a * jax.nn.sigmoid(g)
    y = causal_depthwise_conv(y, conv_w)
    y = layernorm(y, ln_g, ln_b)
    return jax.nn.silu(y)

def mixer_multiscale_pool(w, pool_w, pool_scale):
    bsz, s, _ = w.shape
    wf = w.astype(jnp.float32)
    cs = jnp.cumsum(wf, axis=1)
    pos = jnp.arange(s, dtype=jnp.int32)
    outs = []
    for gi, k in enumerate(POOL_WINDOWS):
        sl = slice(gi * GROUP_DIM, (gi + 1) * GROUP_DIM)
        csg = cs[:, :, sl]
        shifted = jnp.pad(csg, ((0, 0), (k, 0), (0, 0)))[:, :s]
        count = jnp.minimum(pos + 1, k).astype(jnp.float32)[None, :, None]
        outs.append((csg - shifted) / count - wf[:, :, sl])
    pooled = jnp.stack(outs, axis=2).astype(w.dtype)
    y = jnp.einsum("bsgc,gcd->bsgd", pooled, pool_w)
    return y.reshape(bsz, s, MIXER_WIDTH) * pool_scale

def cross_attention(h, m, wq, wkv, wo):
    bsz, s, _ = h.shape
    q = (h @ wq).reshape(bsz, s, N_XATTN_HEADS, XATTN_HEAD_DIM)
    k, v = jnp.split(m @ wkv, 2, axis=-1)
    k = k.reshape(bsz, N_MEM, N_XATTN_HEADS, XATTN_HEAD_DIM)
    v = v.reshape(bsz, N_MEM, N_XATTN_HEADS, XATTN_HEAD_DIM)
    scores = jnp.einsum("bshd,bmhd->bhsm", q, k).astype(jnp.float32) / math.sqrt(XATTN_HEAD_DIM)
    p = jax.nn.softmax(scores, axis=-1).astype(v.dtype)
    o = jnp.einsum("bhsm,bmhd->bshd", p, v).reshape(bsz, s, D_MODEL)
    return o @ wo

def setup_inputs(seed: int = 0) -> dict:
    key = jax.random.key(seed)
    ks = iter(jax.random.split(key, 32))
    L, D, W = DEPTH, D_MODEL, MIXER_WIDTH

    def nrm(shape, fan_in):
        return jax.random.normal(next(ks), shape, jnp.float32) * (fan_in ** -0.5)

    def gain(shape):
        return 1.0 + 0.02 * jax.random.normal(next(ks), shape, jnp.float32)

    def small(shape):
        return 0.02 * jax.random.normal(next(ks), shape, jnp.float32)

    return {
        "x": jax.random.normal(next(ks), (BATCH, SEQ, D), jnp.float32),
        "mem": jax.random.normal(next(ks), (BATCH, N_MEM, D), jnp.float32),
        "norm_ffn1": gain((L, D)),
        "ffn1_w_in": nrm((L, D, 2 * D_FF), D),
        "ffn1_w_out": nrm((L, D_FF, D), D_FF),
        "norm_mix": gain((L, D)),
        "mix_w_in": nrm((L, D, D_IN_PROJ), D),
        "sconv_w": nrm((L, SCONV_K, W), SCONV_K),
        "sgu_norm_g": gain((L, W)),
        "sgu_w": nrm((L, GROUPS_PER_MIXER, SGU_CHUNK, SGU_CHUNK), SGU_CHUNK),
        "sgu_b": gain((L, GROUPS_PER_MIXER, SGU_CHUNK)),
        "cconv_w": nrm((L, CCONV_K, W), CCONV_K),
        "cconv_ln_g": gain((L, W)),
        "cconv_ln_b": small((L, W)),
        "pool_w": nrm((L, len(POOL_WINDOWS), GROUP_DIM, GROUP_DIM), GROUP_DIM),
        "pool_scale": gain((L, W)),
        "mix_w_out": nrm((L, D_MIX, D), D_MIX),
        "norm_xattn": gain((L, D)),
        "norm_mem": gain((L, D)),
        "xattn_wq": nrm((L, D, D), D),
        "xattn_wkv": nrm((L, D, 2 * D), D),
        "xattn_wo": nrm((L, D, D), D),
        "norm_ffn2": gain((L, D)),
        "ffn2_w_in": nrm((L, D, 2 * D_FF), D),
        "ffn2_w_out": nrm((L, D_FF, D), D_FF),
        "norm_final": gain((D,)),
    }

def reference(x, mem, norm_ffn1, ffn1_w_in, ffn1_w_out, norm_mix, mix_w_in, sconv_w,
              sgu_norm_g, sgu_w, sgu_b, cconv_w, cconv_ln_g, cconv_ln_b, pool_w, pool_scale,
              mix_w_out, norm_xattn, norm_mem, xattn_wq, xattn_wkv, xattn_wo,
              norm_ffn2, ffn2_w_in, ffn2_w_out, norm_final):
    W = MIXER_WIDTH
    split_points = [W, 2 * W, 3 * W, 4 * W, 5 * W, 6 * W, 7 * W]
    for l in range(DEPTH):
        x = x + 0.5 * swiglu_ffn(rmsnorm(x, norm_ffn1[l]), ffn1_w_in[l], ffn1_w_out[l])

        h = rmsnorm(x, norm_mix[l])
        z = h @ mix_w_in[l]
        a_b, a_c, a_x, b_u, b_v, c_a, c_g, d_w = jnp.split(z, split_points, axis=-1)
        y_a = mixer_short_conv(a_b, a_c, a_x, sconv_w[l])
        y_b = mixer_spatial_gating(b_u, b_v, sgu_norm_g[l], sgu_w[l], sgu_b[l])
        y_c = mixer_conformer_conv(c_a, c_g, cconv_w[l], cconv_ln_g[l], cconv_ln_b[l])
        y_d = mixer_multiscale_pool(d_w, pool_w[l], pool_scale[l])
        y = jnp.concatenate([y_a, y_b, y_c, y_d], axis=-1)
        x = x + y @ mix_w_out[l]

        x = x + cross_attention(rmsnorm(x, norm_xattn[l]), rmsnorm(mem, norm_mem[l]),
                                xattn_wq[l], xattn_wkv[l], xattn_wo[l])

        x = x + 0.5 * swiglu_ffn(rmsnorm(x, norm_ffn2[l]), ffn2_w_in[l], ffn2_w_out[l])
    return rmsnorm(x, norm_final)


_drawn_inputs = setup_inputs


def setup_inputs(seed=0):
    import zlib

    import numpy as np

    out = dict(_drawn_inputs(seed))
    spreads = {}
    factors = {'norm_ffn1': 4.308,
     'sgu_norm_g': 8.0,
     'sgu_b': 5.839,
     'cconv_ln_g': 8.0,
     'cconv_ln_b': 8.0,
     'pool_scale': 6.34,
     'norm_xattn': 8.0,
     'norm_mem': 8.0,
     'norm_ffn2': 6.785,
     'norm_final': 2.798}
    for name, (base, spread) in spreads.items():
        noise = np.random.default_rng([zlib.crc32(name.encode()), seed]).standard_normal(out[name].shape)
        drawn = base * np.exp(spread * noise) if base else spread * noise
        out[name] = __import__('jax').numpy.asarray(drawn.astype(out[name].dtype))
    for name, factor in factors.items():
        out[name] = (out[name] * factor).astype(out[name].dtype)
    return out
```

```python
from contextlib import ExitStack

import concourse.bass as bass
from concourse import mybir

F32 = mybir.dt.float32
F32R = mybir.dt.float32r
ACT = mybir.ActivationFunctionType
ALU = mybir.AluOpType
AX = mybir.AxisListType

P = 128
EPS = 1e-6
SLOTS = 3
GK = 4
GN = 512
DVE_STEPS = 92


def trunk_kernel(nc, x, mem, norm_ffn1, ffn1_w_in, ffn1_w_out, norm_mix, mix_w_in, sconv_w, sgu_norm_g,
                 sgu_w, sgu_b, cconv_w, cconv_ln_g, cconv_ln_b, pool_w, pool_scale, mix_w_out, norm_xattn,
                 norm_mem, xattn_wq, xattn_wkv, xattn_wo, norm_ffn2, ffn2_w_in, ffn2_w_out, norm_final, out):
    _, S, D = x.shape
    L, _, FF2 = ffn1_w_in.shape
    FF = FF2 // 2
    T = S // P
    KT = D // P
    FT = FF // P
    W = sconv_w.shape[2]
    HC = W
    FC = FF // HC
    TAPS_A, TAPS_C = sconv_w.shape[1], cconv_w.shape[1]
    HEADS = 4
    HD = D // HEADS
    SCALE = float(HD) ** -0.5
    assert T == 2 and KT == 8 and FT == 22 and FC == 11 and W == 256 and HD == 256 and L == 2

    U_F1I = 0
    U_F1O = U_F1I + 2 * FC
    NGO = (FT + GK - 1) // GK
    U_MI = U_F1O + 2 * NGO
    U_K = U_MI + 8
    U_V0 = U_K + 4
    U_MO = U_V0 + 2
    U_Q = U_MO + 4
    U_V1 = U_Q + 4
    U_V = (U_V0, U_V1)
    U_WO = U_V1 + 2
    U_F2I = U_WO + 4
    U_F2O = U_F2I + 2 * FC
    UNITS = U_F2O + 2 * NGO
    assert UNITS % SLOTS == 0
    A_B, A_C, A_X, B_U, B_V, C_A, C_G, D_W = [W * i for i in range(8)]
    MI_COLS = [(C_A, C_G), (A_C, A_X), (A_B, D_W), (B_U, B_V)]

    def unit_kt(u):
        for base in (U_F1O, U_F2O):
            if base <= u < base + 2 * NGO and (u - base) % NGO == NGO - 1:
                return FT - GK * (NGO - 1)
        return GK

    part = [(n, t) for n in range(2) for t in range(T)]
    T_ORDER = ([f"start1{t}" for t in range(T)] + [f"f1_{c}" for c in range(FC)] + [f"mi{n}{t}" for n, t in part]
               + ["glu", "am", "b", "w", "u", "k00", "k01", "k10", "k11", "conv", "norm"]
               + [f"q_in{n}{t}" for n, t in part] + ["q00", "q01", "q10", "q11"]
               + ["p0", "p1", "p2", "p3", "o0", "o1", "o2", "o3"]
               + [f"f2in{n}{t}" for n, t in part] + [f"f2_{c}" for c in range(FC)]
               + [f"next0{t}" for t in range(T)])
    T_LAYER = len(T_ORDER)
    T_AT = {name: i for i, name in enumerate(T_ORDER)}
    T_PRO = 10
    T_AT["start00"], T_AT["start01"] = 1 - T_PRO, 2 - T_PRO
    TB = {name: i % 2 for i, name in enumerate(x for x in T_ORDER if x[:3] not in ("f1_", "f2_"))}
    TB["next00"], TB["next01"] = 0, 1
    TB["start00"], TB["start01"] = 1, 0

    def T_BANK(c):
        return (0, 1, 0)[c % 3]

    F1O_PAIR, F2O_PAIR = (2, 0), (2, 1)
    KPAIR, SGU_PAIR, POOL_PAIR, MO_PAIR, QPAIR, SPAIR, VPAIR, OPAIR, WO_PAIR = 2, 0, 1, (1, 2), (0, 1), (2, 1), (0, 0), (2, 0), (1, 2)

    G_FFN1, G_MIX, G_XATTN, G_MEM, G_FFN2 = range(5)
    ROWS_C = TAPS_A + TAPS_C + 4
    R_SCONV, R_CCONV, R_SGU, R_LNG, R_LNB, R_PS = 0, TAPS_A, TAPS_A + TAPS_C, TAPS_A + TAPS_C + 1, TAPS_A + TAPS_C + 2, TAPS_A + TAPS_C + 3
    N_PAR = 5 * KT + 2 * ROWS_C

    with ExitStack() as ctx:
        def sb(name, shape, dt=F32):
            return ctx.enter_context(nc.sbuf_tensor(name, shape, dt))

        def sem(name):
            return ctx.enter_context(nc.semaphore(name))

        w_raw = sb("w_raw", [P, SLOTS, GK * GN])
        w_hi = sb("w_hi", [P, SLOTS, GK * GN], F32R)
        w_lo = sb("w_lo", [P, SLOTS, GK * GN], F32R)
        xs = sb("xs", [P, T, D])
        xT_hi = sb("xT_hi", [P, KT, S], F32R)
        xT_lo = sb("xT_lo", [P, KT, S], F32R)
        hT_hi = sb("hT_hi", [P, FT, S], F32R)
        hT_lo = sb("hT_lo", [P, FT, S], F32R)
        MEM_KT, Y_KT = 0, KT
        memT = sb("memT", [P, KT, S])
        kT = sb("kT", [P, KT, S])
        xg = sb("xg", [P, T, GN])
        gate = sb("gate", [P, T, HC])
        hact = sb("hact", [P, T, HC])
        ARENA = 6304
        arena = sb("arena", [P, ARENA])
        sq_junk = arena[:, ARENA - GN:]
        par_all = sb("par_all", [P, L + 1, N_PAR])
        par = sb("par", [P, N_PAR])
        poolw_all = sb("poolw_all", [P, L, 2, P])
        poolw = sb("poolw", [P, 2, P])
        sguT = sb("sguT", [P, L, 4, P])
        sgub = sb("sgub", [P, L, 2, P])
        inv_count = sb("inv_count", [P, 2, S])
        ident = sb("ident", [P, P])
        sumsq = sb("sumsq", [P, 2, T])
        var = sb("var", [P, 8, T])
        rstd = sb("rstd", [P, 8, T])
        mhalf = sb("mhalf", [P, T])
        bn6 = sb("bn6", [P, T, 6])
        bn2 = sb("bn2", [P, T, 2])
        smax = sb("smax", [P, HEADS, T])
        nmax = sb("nmax", [P, HEADS, T])
        psum_rows = sb("psum_rows", [P, HEADS, T])
        rinv = sb("rinv", [P, HEADS, T])
        V_MEM, V_X, V_MIX, V_SGU, V_CLN, V_Q, V_F2 = range(7)

        def cut(at, *shape):
            n = 1
            for s in shape:
                n *= s
            v = arena[:, at:at + n]
            if len(shape) == 2:
                v = v.rearrange("p (a b) -> p a b", a=shape[0])
            return v, at + n
        PAD_C, PAD_A, PAD_D = TAPS_C - 1, TAPS_A - 1, 16
        at = 0
        gluT, at = cut(at, 2, PAD_C + S)
        cacc, at = cut(at, 2, S)
        amT, at = cut(at, 2, PAD_A + S)
        aconv, at = cut(at, 2, S)
        zbd, at = cut(at, T, GN)
        wT, at = cut(at, 2, PAD_D + S)
        sumA, at = cut(at, 2, PAD_D + S)
        sumB, at = cut(at, 2, PAD_D + S)
        zuv, at = cut(at, T, GN)
        sg, at = cut(at, 2, S)
        y32 = aconv
        assert at <= ARENA, at
        at = 0
        v1, at = cut(at, T, GN)
        qT, at = cut(at, KT, S)
        probs, at = cut(at, HEADS * T, S)
        kq, at = cut(at, T, GN)
        assert at <= ARENA
        v_half = [sb("v0", [P, T, GN]), v1]
        pT = [qT[:, 2 * h:2 * h + 2, :] for h in range(HEADS)]
        attn = [kq[:, h, :].rearrange("p (t d) -> p t d", t=T) for h in range(2)]
        kbuf = zbd
        at = 0
        mem_sb, at = cut(at, T, D)
        rows_g, at = cut(at, D)
        rows_c, at = cut(at, W)
        sgu_raw, at = cut(at, L * 4, P)
        cnt_a, at = cut(at, S)

        acc = [[ctx.enter_context(nc.psum_tensor(f"acc{p}{t}", [P, GN], F32)) for t in range(T)] for p in range(3)]
        tb = [ctx.enter_context(nc.psum_tensor(f"turn{b}", [P, GN], F32)) for b in range(2)]

        x_landed, mem_landed, rowsg_landed, rowsc_landed, sgu_landed, poolw_landed, gf_landed = [
            sem(n) for n in ("x_landed", "mem_landed", "rowsg_landed", "rowsc_landed", "sgu_landed", "poolw_landed", "gf_landed")]
        sgub_landed = sem("sgub_landed")
        w_landed = [sem(f"w_landed{i}") for i in range(SLOTS)]
        w_split_hi, w_split = sem("w_split_hi"), sem("w_split")
        unit_done = sem("unit_done")
        consts_ready, pads_ready, layer_params = sem("consts_ready"), sem("pads_ready"), sem("layer_params")
        par_ready, sguT_ready, memT_ready = sem("par_ready"), sem("sguT_ready"), sem("memT_ready")
        turned = sem("turned")
        x_updated, x_squared = sem("x_updated"), sem("x_squared")
        var_ready, rstd_ready = sem("var_ready"), sem("rstd_ready")
        xg_ready, xT_hi_ready, xT_ready = sem("xg_ready"), sem("xT_hi_ready"), sem("xT_ready")
        gate_ready, hact_ready = sem("gate_ready"), sem("hact_ready")
        hT_hi_ready, hT_ready = sem("hT_hi_ready"), sem("hT_ready")
        mT_gained, mT_hi_ready, mT_ready = sem("mT_gained"), sem("mT_hi_ready"), sem("mT_ready")
        glu_ready, gluT_ready, conv_ready = sem("glu_ready"), sem("gluT_ready"), sem("conv_ready")
        conv_begun, aconv_begun = sem("conv_begun"), sem("aconv_begun")
        cgate_ready, ac_ready = sem("cgate_ready"), sem("ac_ready")
        cnorm_ready = sem("cnorm_ready")
        am_ready, amT_ready, zbd_ready, wT_ready = sem("am_ready"), sem("amT_ready"), sem("zbd_ready"), sem("wT_ready")
        zuv_ready, vhat_ready, sgu_done, pooled_ready, pool_done = [
            sem(n) for n in ("zuv_ready", "vhat_ready", "sgu_done", "pooled_ready", "pool_done")]
        y32_ready, y_hi_ready, y_ready = sem("y32_ready"), sem("y_hi_ready"), sem("y_ready")
        k_ready, kT_ready, q_ready, qT_ready, v_ready = [sem(n) for n in ("k_ready", "kT_ready", "q_ready", "qT_ready", "v_ready")]
        scores_done, nmax_ready, probs_ready, pT_ready = [sem(n) for n in ("scores_done", "nmax_ready", "probs_ready", "pT_ready")]
        pv_done, rinv_ready, attn_ready, oT_hi_ready, oT_ready = [
            sem(n) for n in ("pv_done", "rinv_ready", "attn_ready", "oT_hi_ready", "oT_ready")]
        dve_step = sem("dve_step")
        passed = sem("passed")
        final_ready, out_landed = sem("final_ready"), sem("out_landed")

        class Layer:
            def __init__(self, l, it=None):
                self.l, self.it = l, it

            def at(self, per_layer, const, per_it=0):
                v = self.l * per_layer + const
                if self.it is not None and per_it:
                    v = v + self.it * per_it
                return v

        class Steps:
            def __init__(self, eng, s, per_layer, base=0):
                self.eng, self.s, self.per_layer, self.base, self.n, self.here = eng, s, per_layer, base, 0, None

            def mark(self, ins):
                ins.then_inc(self.s, 1)
                self.n += 1
                return self.n

            def wait(self, n):
                if self.here is None:
                    self.eng.wait_ge(self.s, n)
                else:
                    self.eng.wait_ge(self.s, self.here.at(self.per_layer, self.base + n))

            def link(self, ins):
                self.wait(self.mark(ins))

        def w_cols(w):
            return w.rearrange("l (a p) n -> l p a n", p=P)

        v_f1i, v_f1o, v_mi, v_mo = w_cols(ffn1_w_in), w_cols(ffn1_w_out), w_cols(mix_w_in), w_cols(mix_w_out)
        v_q, v_kv, v_wo = w_cols(xattn_wq), w_cols(xattn_wkv), w_cols(xattn_wo)
        v_f2i, v_f2o = w_cols(ffn2_w_in), w_cols(ffn2_w_out)

        block = ctx.enter_context(nc.Block())

        @block.sync
        def _(sp):
            sp.dma_start(xs[:, :, :], x.rearrange("o (t p) d -> p (o t) d", p=P)).then_inc(x_landed, 16)
            for w, g in ((G_FFN1, norm_ffn1), (G_MIX, norm_mix), (G_XATTN, norm_xattn)):
                sp.dma_start(rows_g[L * w:L * w + L, :], g).then_inc(rowsg_landed, 16)
            sp.dma_start(mem_sb, mem.rearrange("o (t p) d -> p (o t) d", p=P)).then_inc(mem_landed, 16)

            def unit(u, at, k, parts):
                sp.wait_ge(w_split, at.at(UNITS, u + 1, k))
                sp.sem_inc(passed, 1)
                for dst, src in parts:
                    sp.dma_start(dst, src).then_inc(w_landed[u % SLOTS], 16)

            def pair_parts(u, src, l, a, c0, c1):
                dst = w_raw[:, u % SLOTS, :].rearrange("p (k n) -> p k n", k=GK)
                return [(dst[:, :, i * HC:(i + 1) * HC],
                         src[bass.ds(l, 1), :, a:a + GK, bass.ds(c, HC)].rearrange("o p k n -> p (o k) n"))
                        for i, c in enumerate((c0, c1))]

            def wide_parts(u, src, l, a, nk, c):
                h = nk // 2
                return [(w_raw[:, u % SLOTS, i * h * GN:(i + 1) * h * GN].rearrange("p (k n) -> p k n", k=h),
                         src[bass.ds(l, 1), :, a + i * h:a + (i + 1) * h, c:c + GN].rearrange("o p k n -> p (o k) n"))
                        for i in range(2)]

            def ffn(l, base, src_in, src_out):
                with sp.Fori(0, 3) as it:
                    at = Layer(l, it)
                    for k in range(3):
                        for j in range(2):
                            u = base + 2 * k + j
                            unit(u, at, 6, pair_parts(u, src_in, l, GK * j, it * (3 * HC) + k * HC, it * (3 * HC) + (k * HC + FF)))
                at = Layer(l)
                for c in range(9, FC):
                    for j in range(2):
                        u = base + 2 * c + j
                        unit(u, at, 0, pair_parts(u, src_in, l, GK * j, c * HC, c * HC + FF))
                for n in range(2):
                    for j in range(NGO):
                        u = base + 2 * FC + n * NGO + j
                        unit(u, at, 0, wide_parts(u, src_out, l, GK * j, unit_kt(u), n * GN))

            with sp.Fori(0, L) as l:
                at = Layer(l)
                ffn(l, U_F1I, v_f1i, v_f1o)
                for i, (c0, c1) in enumerate(MI_COLS):
                    for j in range(2):
                        u = U_MI + 2 * i + j
                        unit(u, at, 0, pair_parts(u, v_mi, l, GK * j, c0, c1))
                for base, src, col, halves in ((U_K, v_kv, 0, 2), (U_V0, v_kv, D, 1), (U_MO, v_mo, 0, 2), (U_Q, v_q, 0, 2),
                                               (U_V1, v_kv, D + GN, 1), (U_WO, v_wo, 0, 2)):
                    for n in range(halves):
                        for j in range(2):
                            u = base + 2 * n + j
                            unit(u, at, 0, wide_parts(u, src, l, GK * j, GK, col + n * GN))
                ffn(l, U_F2I, v_f2i, v_f2o)
            sp.wait_ge(mT_ready, L * 4)
            sp.dma_start(memT[:, 0:4, :].rearrange("p k s -> p (k s)"),
                         norm_final.rearrange("(o d) -> o d", o=1).to_broadcast([P, D])).then_inc(gf_landed, 16)
            sp.wait_ge(w_split, L * UNITS + SLOTS)
            sp.sem_inc(w_landed[0], 32)
            sp.sem_inc(w_landed[1], 32)
            for t in range(T):
                sp.wait_ge(final_ready, t + 1)
                sp.dma_start(out[0, t * P:(t + 1) * P, :], xs[:, t, :]).then_inc(out_landed, 16)
            sp.wait_ge(out_landed, 16 * T)

        @block.gpsimd
        def _(pool):
            pool.memset(ident[:, :], 0.0).then_inc(pads_ready, 1)
            pool.memset(poolw_all[:, :, :, :], 0.0).then_inc(pads_ready, 1)
            pool.wait_ge(pads_ready, 2)
            pool.affine_select(out=ident[:, :], in_=ident[:, :], compare_op=ALU.not_equal, fill=1.0, base=0,
                               pattern=[[-1, P]], channel_multiplier=1).then_inc(consts_ready, 1)
            pool.memset(mhalf[:, :], -0.5).then_inc(pads_ready, 1)
            pool.wait_ge(sgu_landed, 16)
            pool.affine_select(out=sgu_raw, in_=sgu_raw, compare_op=ALU.is_ge, fill=0.0, base=0,
                               pattern=[[0, L * 4], [-1, P]], channel_multiplier=1).then_inc(consts_ready, 1)
            pool.wait_ge(pads_ready, 3)

            def inv_sqrt(n, i, v):
                pool.wait_ge(var_ready, n)
                pool.tensor_tensor(rstd[:, i, :], var[:, i, :], mhalf[:, :], ALU.pow).then_inc(rstd_ready, 1)

            inv_sqrt(1, V_X, 0)
            inv_sqrt(2, V_MEM, 0)
            pool.wait_ge(poolw_landed, 32)
            pool.wait_ge(sgub_landed, 32)
            pool.wait_ge(par_ready, 2)
            with pool.Fori(0, L) as l:
                at = Layer(l)
                pool.wait_ge(x_updated, at.at(16, T))
                pool.tensor_copy(par[:, :], par_all[:, bass.ds(l, 1), :].rearrange("p o n -> p (o n)")).then_inc(layer_params, 1)
                pool.tensor_copy(poolw[:, :, :], poolw_all[:, bass.ds(l, 1), :, :].rearrange("p o c d -> p (o c) d")).then_inc(layer_params, 1)
                for k, i in enumerate((V_MIX, V_SGU, V_CLN, V_Q, V_F2, V_X)):
                    inv_sqrt(at.at(6, 3 + k), i, 0)

        @block.scalar
        def _(act):
            for w, g in ((G_MEM, norm_mem), (G_FFN2, norm_ffn2)):
                act.dma_start(rows_g[L * w:L * w + L, :], g).then_inc(rowsg_landed, 16)
            for at_r, src in ((R_SCONV, sconv_w.rearrange("l j c -> (l j) c")), (R_CCONV, cconv_w.rearrange("l j c -> (l j) c")),
                              (R_SGU, sgu_norm_g), (R_LNG, cconv_ln_g), (R_LNB, cconv_ln_b), (R_PS, pool_scale)):
                act.dma_start(rows_c[L * at_r:L * at_r + src.shape[0], :], src).then_inc(rowsc_landed, 16)
            act.dma_start(sgu_raw, sgu_w.rearrange("l h t s -> t (l h) s")).then_inc(sgu_landed, 16)
            state = {"next": 0}

            def split_hi(u, at, k=0):
                n = unit_kt(u) * GN
                act.wait_ge(w_landed[u % SLOTS], at.at(32 * (UNITS // SLOTS), 32 * (u // SLOTS + 1), 32 * k // SLOTS))
                act.wait_ge(unit_done, at.at(2 * UNITS, 2 * u + 2, 2 * k))
                act.copy(w_hi[:, u % SLOTS, 0:n], w_raw[:, u % SLOTS, 0:n]).then_inc(w_split_hi, 1)

            def weights_to(u, at):
                while state["next"] <= u:
                    split_hi(state["next"], at)
                    state["next"] += 1

            def square(src, n, t, before):
                act.wait_ge(x_squared, before) if not isinstance(before, int) or before else None
                act.activation(sq_junk, src[:, t, n * GN:(n + 1) * GN], ACT.Square,
                               accum_out=sumsq[:, n, t:t + 1]).then_inc(x_squared, 1)

            def xT_hi_part(b, n, t, at):
                act.wait_ge(xg_ready, at.at(16, 4 * b + 2 * n + t + 1))
                act.copy(xT_hi[:, 4 * n:4 * n + 4, t * P:(t + 1) * P],
                         xg[:, t, :].rearrange("p (k s) -> p k s", k=4)).then_inc(xT_hi_ready, 1)

            act.wait_ge(x_landed, 16)
            for i, (n, t) in enumerate(part):
                if n:
                    xT_hi_part(0, 0, t, Layer(0))
                square(xs, n, t, i)
            act.wait_ge(mem_landed, 16)
            act.wait_ge(var_ready, 1)
            for i, (n, t) in enumerate(part):
                square(mem_sb, n, t, 4 + i)
            weights_to(1, Layer(0))
            for f in range(2):
                act.dma_start(sgub[64 * f:64 * f + 64, :, :, :].rearrange("p l c t -> p (l c) t"),
                              sgu_b.rearrange("l (c f) t -> f (l c) t", f=2)[f:f + 1].to_broadcast([64, 2 * L, P])).then_inc(sgub_landed, 16)
            act.wait_ge(pads_ready, 2)
            for f in range(2):
                act.dma_start(poolw_all[64 * f:64 * f + 64, :, :, 64 * f:64 * f + 64].rearrange("p l c d -> p (l c) d"),
                              pool_w.rearrange("l (c f) p d -> f p (l c) d", f=2)[f]).then_inc(poolw_landed, 16)

            def squares(b, n, at):
                for t in range(T):
                    act.wait_ge(x_updated, at.at(16, T + 4 * b + 2 * n + t + 1))
                    square(xs, n, t, at.at(16, 8 + 4 * b + 2 * n + t))

            def ffn(l, base, f):
                def chunk(c, at, loop):
                    k = 6 if loop else 0
                    for t in range(T):
                        act.wait_ge(unit_done, at.at(2 * UNITS, 2 * SLOTS + 2 * (base + 2 * c + 1) + t + 1, 2 * k))
                        act.wait_ge(hact_ready, at.at(4 * FC, 2 * FC * f + 2 * c + t + 1, k))
                        act.activation(gate[:, t, :], acc[c % 3][t][:, 0:HC], ACT.Silu,
                                       scale=rstd[:, V_F2 if f else V_X, t:t + 1]).then_inc(gate_ready, 1)
                    split_hi(base + 2 * c + 4, at, k)
                    act.wait_ge(turned, at.at(T_LAYER, T_PRO + T_AT[f"f{f + 1}_0"] + c + 1, k // 2))
                    act.copy(hT_hi[:, 2 * c:2 * c + 2, :] if not loop else hT_hi[:, bass.ds(at.it * 6 + 2 * c, 2), :],
                             tb[T_BANK(c)][:, :].rearrange("p (k s) -> p k s", k=2)).then_inc(hT_hi_ready, 1)
                    split_hi(base + 2 * c + 5, at, k)

                with act.Fori(0, 3) as it:
                    for c in range(3):
                        chunk(c, Layer(l, it), True)
                for c in range(9, FC):
                    chunk(c, Layer(l), False)
                state["next"] = base + 2 * FC + 4

            with act.Fori(0, L) as l:
                at = Layer(l)
                state["next"] = 2
                xT_hi_part(0, 1, 0, at)
                weights_to(2, at)
                xT_hi_part(0, 1, 1, at)
                weights_to(3, at)
                act.wait_ge(rstd_ready, at.at(6, 2))
                ffn(l, U_F1I, 0)

                weights_to(U_F1O + 7, at)
                squares(0, 0, at)
                weights_to(U_F1O + 8, at)
                xT_hi_part(1, 0, 0, at)
                weights_to(U_F1O + 9, at)
                xT_hi_part(1, 0, 1, at)
                weights_to(U_MI + 1, at)
                squares(0, 1, at)
                xT_hi_part(1, 1, 0, at)
                weights_to(U_MI + 2, at)
                xT_hi_part(1, 1, 1, at)

                def mT_hi_part(i):
                    if i >= 2:
                        act.wait_ge(mT_ready, at.at(4, i - 1))
                    for k in range(2):
                        g = G_MEM * KT + 2 * i + k
                        act.activation(xg[:, i % 2, k * S:(k + 1) * S], memT[:, 2 * i + k, :], ACT.Copy,
                                       scale=par[:, g:g + 1]).then_inc(mT_gained, 1)
                    act.wait_ge(mT_gained, at.at(8, 2 * i + 2))
                    act.copy(hT_hi[:, MEM_KT + 2 * i:MEM_KT + 2 * i + 2, :],
                             xg[:, i % 2, :].rearrange("p (k s) -> p k s", k=2)).then_inc(mT_hi_ready, 1)

                def y_hi(i, kt, buf):
                    act.wait_ge(y32_ready, at.at(4, i + 1))
                    act.copy(hT_hi[:, Y_KT + kt:Y_KT + kt + 2, :], buf).then_inc(y_hi_ready, 1)

                def evac(u, t):
                    act.wait_ge(unit_done, at.at(2 * UNITS, 2 * SLOTS + 2 * u + t + 1))

                def first_taps(src, sums, r, src_ready, begun):
                    act.wait_ge(src_ready, at.at(1, 1))
                    for ct in range(2):
                        o = 5 * KT + ct * ROWS_C + r
                        ins = act.activation(sums[:, ct, :], src[:, ct, 0:S], ACT.Copy, scale=par[:, o:o + 1])
                    ins.then_inc(begun, 1)

                weights_to(U_MI + 3, at)
                act.wait_ge(xT_ready, at.at(16, 8))
                mT_hi_part(0)
                weights_to(U_MI + 4, at)
                act.wait_ge(rstd_ready, at.at(6, 3))
                for t in range(T):
                    evac(U_MI + 1, t)
                    act.activation(gate[:, t, :], acc[1][t][:, HC:GN], ACT.Sigmoid,
                                   scale=rstd[:, V_MIX, t:t + 1]).then_inc(cgate_ready, 1)
                mT_hi_part(1)
                weights_to(U_MI + 5, at)
                act.wait_ge(turned, at.at(T_LAYER, T_PRO + T_AT["glu"] + 1))
                act.copy(gluT[:, :, PAD_C:], tb[0][:, :].rearrange("p (c s) -> p c s", c=2)).then_inc(gluT_ready, 1)
                first_taps(gluT, cacc, R_CCONV, gluT_ready, conv_begun)
                mT_hi_part(2)
                mT_hi_part(3)
                weights_to(U_MI + 6, at)
                for t in range(T):
                    evac(U_MI + 3, t)
                    act.activation(gate[:, t, :], acc[2][t][:, 0:HC], ACT.Copy,
                                   scale=rstd[:, V_MIX, t:t + 1]).then_inc(ac_ready, 1)
                weights_to(U_MI + 7, at)
                act.wait_ge(turned, at.at(T_LAYER, T_PRO + T_AT["am"] + 1))
                act.copy(amT[:, :, PAD_A:], tb[1][:, :].rearrange("p (c s) -> p c s", c=2)).then_inc(amT_ready, 1)
                first_taps(amT, aconv, R_SCONV, amT_ready, aconv_begun)
                weights_to(U_K, at)
                for t in range(T):
                    evac(U_MI + 5, t)
                    act.activation(zbd[:, t, :], acc[0][t][:, :], ACT.Copy,
                                   scale=rstd[:, V_MIX, t:t + 1]).then_inc(zbd_ready, 1)
                weights_to(U_K + 1, at)
                act.wait_ge(turned, at.at(T_LAYER, T_PRO + T_AT["w"] + 1))
                act.copy(wT[:, :, PAD_D:], tb[1][:, :].rearrange("p (c s) -> p c s", c=2)).then_inc(wT_ready, 1)
                for t in range(T):
                    evac(U_MI + 7, t)
                    act.activation(zuv[:, t, :], acc[1][t][:, :], ACT.Copy,
                                   scale=rstd[:, V_MIX, t:t + 1]).then_inc(zuv_ready, 1)
                weights_to(U_K + 2, at)
                y_hi(0, 0, y32)
                weights_to(U_K + 3, at)
                act.wait_ge(rstd_ready, 1)

                def keys(n):
                    for t in range(T):
                        evac(U_K + 2 * n + 1, t)
                        if n == 1:
                            act.wait_ge(turned, at.at(T_LAYER, T_PRO + T_AT["k01"] + 1))
                        act.activation(kbuf[:, t, :], acc[KPAIR][t][:, :], ACT.Copy,
                                       scale=rstd[:, V_MEM, t:t + 1]).then_inc(k_ready, 1)

                def key_turn(n):
                    for t in range(T):
                        act.wait_ge(turned, at.at(T_LAYER, T_PRO + T_AT[f"k{n}{t}"] + 1))
                        act.copy(kT[:, 4 * n:4 * n + 4, t * P:(t + 1) * P],
                                 tb[TB[f"k{n}{t}"]][:, :].rearrange("p (k s) -> p k s", k=4)).then_inc(kT_ready, 1)

                def values(n):
                    for t in range(T):
                        evac(U_V[n] + 1, t)
                        act.activation(v_half[n][:, t, :], acc[VPAIR[n]][t][:, :], ACT.Copy,
                                       scale=rstd[:, V_MEM, t:t + 1]).then_inc(v_ready, 1)

                keys(0)
                weights_to(U_V0, at)
                y_hi(1, 2, y32)
                act.wait_ge(pool_done, at.at(1, 1))
                act.wait_ge(y_ready, at.at(4, 2))
                for ct in range(2):
                    o = 5 * KT + ct * ROWS_C + R_PS
                    ins = act.activation(y32[:, ct, :], acc[POOL_PAIR][ct][:, 0:S], ACT.Copy, scale=par[:, o:o + 1])
                ins.then_inc(y32_ready, 1)
                y_hi(2, 6, y32)
                key_turn(0)
                weights_to(U_V0 + 1, at)
                keys(1)
                weights_to(U_MO, at)
                key_turn(1)
                weights_to(U_MO + 1, at)
                values(0)
                weights_to(U_MO + 2, at)
                act.wait_ge(turned, at.at(T_LAYER, T_PRO + T_AT["norm"] + 1))
                act.wait_ge(y_ready, at.at(4, 3))
                for ct in range(2):
                    o = 5 * KT + ct * ROWS_C
                    ins = act.activation(y32[:, ct, :], tb[TB["norm"]][:, ct * S:(ct + 1) * S], ACT.Silu,
                                         scale=par[:, o + R_LNG:o + R_LNG + 1], bias=par[:, o + R_LNB:o + R_LNB + 1])
                ins.then_inc(y32_ready, 1)
                y_hi(3, 4, y32)
                weights_to(U_MO + 3, at)

                def boundary(u_end, b, extra=None):
                    weights_to(u_end + 2, at)
                    squares(b, 0, at)
                    weights_to(u_end + 3, at)
                    xT_hi_part(b + 1, 0, 0, at)
                    xT_hi_part(b + 1, 0, 1, at)
                    weights_to(u_end + 4, at)
                    squares(b, 1, at)
                    xT_hi_part(b + 1, 1, 0, at)
                    weights_to(u_end + 5, at)
                    xT_hi_part(b + 1, 1, 1, at)

                boundary(U_MO + 1, 1)
                act.wait_ge(rstd_ready, at.at(6, 6))

                def queries(n):
                    for t in range(T):
                        evac(U_Q + 2 * n + 1, t)
                        if n == 1:
                            act.wait_ge(turned, at.at(T_LAYER, T_PRO + T_AT["q01"] + 1))
                        act.activation(kq[:, t, :], acc[QPAIR[n]][t][:, :], ACT.Copy,
                                       scale=rstd[:, V_Q, t:t + 1]).then_inc(q_ready, 1)

                def query_turn(n):
                    for t in range(T):
                        act.wait_ge(turned, at.at(T_LAYER, T_PRO + T_AT[f"q{n}{t}"] + 1))
                        act.copy(qT[:, 4 * n:4 * n + 4, t * P:(t + 1) * P],
                                 tb[TB[f"q{n}{t}"]][:, :].rearrange("p (k s) -> p k s", k=4)).then_inc(qT_ready, 1)

                def exps(h):
                    act.wait_ge(nmax_ready, at.at(HEADS, h + 1))
                    for t in range(T):
                        act.activation(probs[:, T * h + t, :], acc[SPAIR[h // 2]][h % 2][:, t * S:(t + 1) * S], ACT.Exp,
                                       bias=nmax[:, h, t:t + 1], scale=SCALE,
                                       accum_out=psum_rows[:, h, t:t + 1]).then_inc(probs_ready, 1)

                weights_to(U_Q + 3, at)
                queries(0)
                weights_to(U_V1, at)
                query_turn(0)
                weights_to(U_V1 + 1, at)
                queries(1)
                exps(0)
                exps(1)
                query_turn(1)
                weights_to(U_WO, at)
                exps(2)
                exps(3)
                weights_to(U_WO + 1, at)
                values(1)
                weights_to(U_WO + 2, at)

                def attn_out(h):
                    act.wait_ge(rinv_ready, at.at(HEADS, h + 1))
                    act.wait_ge(pv_done, at.at(HEADS, h + 1))
                    if h >= 2:
                        act.wait_ge(turned, at.at(T_LAYER, T_PRO + T_AT[f"o{h - 2}"] + 1))
                    for t in range(T):
                        ins = act.activation(attn[h % 2][:, t, :], acc[OPAIR[h // 2]][h % 2][:, t * S:(t + 1) * S], ACT.Copy,
                                             scale=rinv[:, h, t:t + 1])
                    ins.then_inc(attn_ready, 1)

                def attn_hi(h):
                    act.wait_ge(turned, at.at(T_LAYER, T_PRO + T_AT[f"o{h}"] + 1))
                    act.copy(hT_hi[:, Y_KT + 2 * h:Y_KT + 2 * h + 2, :],
                             tb[TB[f"o{h}"]][:, :].rearrange("p (k s) -> p k s", k=2)).then_inc(oT_hi_ready, 1)

                attn_out(0)
                attn_out(1)
                attn_hi(0)
                attn_out(2)
                attn_hi(1)
                attn_out(3)
                attn_hi(2)
                attn_hi(3)

                boundary(U_WO + 1, 2)
                weights_to(U_F2I + 3, at)
                act.wait_ge(rstd_ready, at.at(6, 7))
                ffn(l, U_F2I, 1)
                weights_to(U_F2O + 7, at)
                squares(3, 0, at)
                weights_to(U_F2O + 8, at)
                xT_hi_part(4, 0, 0, at)
                weights_to(U_F2O + 9, at)
                xT_hi_part(4, 0, 1, at)
                weights_to(UNITS + 1, at)
                squares(3, 1, at)

        @block.vector
        def _(dve):
            dve.sem_inc(w_split, SLOTS)
            dve.sem_inc(hact_ready, T)
            dve.sem_inc(hT_ready, 1)
            steps = Steps(dve, dve_step, DVE_STEPS)
            state = {"next": 0}

            def split_lo(u, at, k=0):
                n = unit_kt(u) * GN
                dve.wait_ge(w_split_hi, at.at(UNITS, u + 1, k))
                dve.tensor_tensor(w_lo[:, u % SLOTS, 0:n], w_raw[:, u % SLOTS, 0:n],
                                  w_hi[:, u % SLOTS, 0:n].bitcast(F32), ALU.subtract).then_inc(w_split, 1)

            def weights_to(u, at):
                while state["next"] <= u:
                    split_lo(state["next"], at)
                    state["next"] += 1

            def gained(b, n, t, g, name, at, layer=None):
                dve.wait_ge(turned, at.at(T_LAYER, T_PRO + T_AT[name] + 1))
                cols = slice(g * KT + 4 * n, g * KT + 4 * n + 4)
                gain = par[:, cols] if layer is None else par_all[:, bass.ds(layer, 1), cols].rearrange("p o k -> p (o k)")
                gain = gain.unsqueeze(2).to_broadcast([P, 4, P])
                dve.tensor_tensor(xg[:, t, :].rearrange("p (k s) -> p k s", k=4),
                                  tb[TB[name]][:, :].rearrange("p (k s) -> p k s", k=4), gain, ALU.mult).then_inc(xg_ready, 1)

            def xT_lo_part(b, n, t, at):
                dve.wait_ge(xT_hi_ready, at.at(16, 4 * b + 2 * n + t + 1))
                cols = slice(t * P, (t + 1) * P)
                dve.tensor_tensor(xT_lo[:, 4 * n:4 * n + 4, cols], xg[:, t, :].rearrange("p (k s) -> p k s", k=4),
                                  xT_hi[:, 4 * n:4 * n + 4, cols].bitcast(F32), ALU.subtract).then_inc(xT_ready, 1)

            def variance(i, chain):
                chain.link(dve.tensor_tensor(var[:, i, :], sumsq[:, 0, :], sumsq[:, 1, :], ALU.add))
                dve.tensor_scalar(var[:, i, :], var[:, i, :], 1.0 / D, EPS, ALU.mult, ALU.add).then_inc(var_ready, 1)

            for ct in range(2):
                for f in range(2):
                    k = 2 << (2 * ct + f)
                    rows = inv_count[64 * f:64 * f + 64, ct, :]
                    dve.memset(rows[:, k - 1:S], 1.0 / k)
                    for t in range(k - 1):
                        ins = dve.memset(rows[:, t:t + 1], 1.0 / (t + 1))
            steps.link(ins)
            dve.memset(par_all[:, L, :], 0.0)
            dve.wait_ge(turned, 1)
            src = tb[0][:, 0:KT * 5 * L].rearrange("p (k w l) -> p l w k", k=KT, l=L)
            for l in range(L):
                ins = dve.tensor_copy(par_all[:, l, 0:5 * KT].rearrange("p (w k) -> p w k", k=KT), src[:, l, :, :])
            ins.then_inc(par_ready, 1)
            dve.wait_ge(par_ready, 1)
            for t in range(T):
                gained(0, 0, t, G_FFN1, f"start0{t}", Layer(0), layer=0)
            for t in range(T):
                xT_lo_part(0, 0, t, Layer(0))
            dve.wait_ge(x_squared, 4)
            variance(V_X, steps)
            dve.wait_ge(turned, 4)
            src = tb[1][:, 0:2 * L * ROWS_C].rearrange("p (c r) -> p c r", c=2)
            dst = par_all[:, :, 5 * KT:].rearrange("p l (c j) -> p l c j", c=2)
            for r, n in ((R_SCONV, TAPS_A), (R_CCONV, TAPS_C), (R_SGU, 1), (R_LNG, 1), (R_LNB, 1), (R_PS, 1)):
                for c in range(2):
                    ins = dve.tensor_copy(dst[:, 0:L, c, r:r + n], src[:, c, L * r:L * (r + n)].rearrange("p (l j) -> p l j", l=L))
            ins.then_inc(par_ready, 1)
            for i, (n, t) in enumerate(part):
                dve.wait_ge(turned, 5 + i)
                dve.tensor_copy(memT[:, 4 * n:4 * n + 4, t * P:(t + 1) * P],
                                tb[i % 2][:, :].rearrange("p (k s) -> p k s", k=4)).then_inc(memT_ready, 1)
            for i in range(2):
                dve.wait_ge(turned, 9 + i)
                dve.tensor_copy(sguT[:, i, :, :].rearrange("p h t -> p (h t)"), tb[i][:, :]).then_inc(sguT_ready, 1)
            dve.wait_ge(x_squared, 8)
            variance(V_MEM, steps)
            weights_to(1, Layer(0))
            dve.wait_ge(x_landed, 16)
            dve.wait_ge(par_ready, 2)
            dve.wait_ge(sguT_ready, 2)
            dve.wait_ge(memT_ready, 4)
            dve.sem_inc(x_updated, T)
            steps.base = steps.n

            def update(b, n, t, u, pair, factor, at):
                dve.wait_ge(unit_done, at.at(2 * UNITS, 2 * SLOTS + 2 * u + t + 1))
                cols = xs[:, t, n * GN:(n + 1) * GN]
                dve.scalar_tensor_tensor(out=cols, in0=acc[pair][t][:, :], scalar=factor, in1=cols,
                                         op0=ALU.mult, op1=ALU.add).then_inc(x_updated, 1)

            def ffn(l, base, f):
                def chunk(c, at, loop):
                    k = 6 if loop else 0
                    for t in range(T):
                        dve.wait_ge(gate_ready, at.at(4 * FC, 2 * FC * f + 2 * c + t + 1, k))
                        dve.scalar_tensor_tensor(out=hact[:, t, :], in0=acc[c % 3][t][:, HC:GN],
                                                 scalar=rstd[:, V_F2 if f else V_X, t:t + 1], in1=gate[:, t, :],
                                                 op0=ALU.mult, op1=ALU.mult).then_inc(hact_ready, 1)
                    split_lo(base + 2 * c + 4, at, k)
                    dve.wait_ge(hT_hi_ready, at.at(2 * FC, FC * f + c + 1, k // 2))
                    rows = slice(2 * c, 2 * c + 2) if not loop else bass.ds(at.it * 6 + 2 * c, 2)
                    dve.tensor_tensor(hT_lo[:, rows, :], tb[T_BANK(c)][:, :].rearrange("p (k s) -> p k s", k=2),
                                      hT_hi[:, rows, :].bitcast(F32), ALU.subtract).then_inc(hT_ready, 1)
                    split_lo(base + 2 * c + 5, at, k)

                with dve.Fori(0, 3) as it:
                    for c in range(3):
                        chunk(c, Layer(l, it), True)
                for c in range(9, FC):
                    chunk(c, Layer(l), False)
                state["next"] = base + 2 * FC + 4

            with dve.Fori(0, L) as l:
                at = Layer(l)
                steps.here, steps.n, state["next"] = at, 0, 2
                for t in range(T):
                    gained(0, 1, t, G_FFN1, f"start1{t}", at, layer=l)
                    xT_lo_part(0, 1, t, at)
                dve.wait_ge(layer_params, at.at(2, 2))
                steps.link(dve.memset(gluT[:, :, 0:PAD_C], 0.0))
                steps.link(dve.memset(amT[:, :, 0:PAD_A], 0.0))
                steps.link(dve.memset(wT[:, :, 0:PAD_D], 0.0))
                weights_to(3, at)
                ffn(l, U_F1I, 0)

                weights_to(U_F1O + 7, at)
                update(0, 0, 0, U_F1O + 5, F1O_PAIR[0], 0.5, at)
                update(0, 0, 1, U_F1O + 5, F1O_PAIR[0], 0.5, at)
                weights_to(U_F1O + 8, at)
                gained(1, 0, 0, G_MIX, "mi00", at)
                weights_to(U_F1O + 9, at)
                xT_lo_part(1, 0, 0, at)
                gained(1, 0, 1, G_MIX, "mi01", at)
                xT_lo_part(1, 0, 1, at)
                weights_to(U_MI, at)
                update(0, 1, 0, U_F1O + 11, F1O_PAIR[1], 0.5, at)
                weights_to(U_MI + 1, at)
                update(0, 1, 1, U_F1O + 11, F1O_PAIR[1], 0.5, at)
                gained(1, 1, 0, G_MIX, "mi10", at)
                xT_lo_part(1, 1, 0, at)
                gained(1, 1, 1, G_MIX, "mi11", at)
                xT_lo_part(1, 1, 1, at)
                dve.wait_ge(x_squared, at.at(16, 8 + 4))
                variance(V_MIX, steps)
                weights_to(U_MI + 2, at)

                def mT_lo_part(i):
                    kt = slice(MEM_KT + 2 * i, MEM_KT + 2 * i + 2)
                    dve.wait_ge(mT_hi_ready, at.at(4, i + 1))
                    dve.tensor_tensor(hT_lo[:, kt, :], xg[:, i % 2, :].rearrange("p (k s) -> p k s", k=2),
                                      hT_hi[:, kt, :].bitcast(F32), ALU.subtract).then_inc(mT_ready, 1)

                def y_lo(i, kt, buf):
                    dve.wait_ge(y_hi_ready, at.at(4, i + 1))
                    rows = slice(Y_KT + kt, Y_KT + kt + 2)
                    dve.tensor_tensor(hT_lo[:, rows, :], buf, hT_hi[:, rows, :].bitcast(F32), ALU.subtract).then_inc(y_ready, 1)

                taps = {"n": 2, "last": [None, None]}

                def conv_taps(count):
                    if taps["n"] == 2:
                        dve.wait_ge(conv_begun, at.at(1, 1))
                    for i in range(taps["n"], min(taps["n"] + count, 2 * TAPS_C)):
                        j, ct = i // 2, i % 2
                        o = 5 * KT + ct * ROWS_C + R_CCONV + j
                        src, tap = gluT[:, ct, j:j + S], par[:, o:o + 1]
                        if j > 1:
                            steps.wait(taps["last"][ct])
                        ins = dve.scalar_tensor_tensor(out=cacc[:, ct, :], in0=src, scalar=tap, in1=cacc[:, ct, :],
                                                       op0=ALU.mult, op1=ALU.add)
                        if i == 2 * TAPS_C - 1:
                            ins.then_inc(conv_ready, 1)
                        else:
                            taps["last"][ct] = steps.mark(ins)
                    taps["n"] += count

                weights_to(U_MI + 3, at)
                mT_lo_part(0)
                weights_to(U_MI + 4, at)
                for t in range(T):
                    dve.wait_ge(cgate_ready, at.at(2, t + 1))
                    dve.scalar_tensor_tensor(out=hact[:, t, :], in0=acc[1][t][:, 0:HC], scalar=rstd[:, V_MIX, t:t + 1],
                                             in1=gate[:, t, :], op0=ALU.mult, op1=ALU.mult).then_inc(glu_ready, 1)
                mT_lo_part(1)
                weights_to(U_MI + 5, at)
                conv_taps(4)
                mT_lo_part(2)
                conv_taps(4)
                mT_lo_part(3)
                weights_to(U_MI + 6, at)
                for t in range(T):
                    dve.wait_ge(ac_ready, at.at(2, t + 1))
                    dve.scalar_tensor_tensor(out=hact[:, t, :], in0=acc[2][t][:, HC:GN], scalar=rstd[:, V_MIX, t:t + 1],
                                             in1=gate[:, t, :], op0=ALU.mult, op1=ALU.mult).then_inc(am_ready, 1)
                conv_taps(8)
                weights_to(U_MI + 7, at)
                conv_taps(8)
                weights_to(U_K, at)
                dve.wait_ge(aconv_begun, at.at(1, 1))
                last = [None, None]
                for j in range(1, TAPS_A):
                    for ct in range(2):
                        o = 5 * KT + ct * ROWS_C + R_SCONV + j
                        src, tap = amT[:, ct, j:j + S], par[:, o:o + 1]
                        if j > 1:
                            steps.wait(last[ct])
                        ins = dve.scalar_tensor_tensor(out=aconv[:, ct, :], in0=src, scalar=tap, in1=aconv[:, ct, :],
                                                       op0=ALU.mult, op1=ALU.add)
                        last[ct] = steps.mark(ins)
                conv_taps(4)
                weights_to(U_K + 1, at)
                dve.wait_ge(turned, at.at(T_LAYER, T_PRO + T_AT["b"] + 1))
                steps.wait(last[1])
                dve.tensor_tensor(y32, aconv, tb[TB["b"]][:, :].rearrange("p (c s) -> p c s", c=2), ALU.mult).then_inc(y32_ready, 1)
                conv_taps(2)
                dve.wait_ge(wT_ready, at.at(1, 1))
                E = PAD_D + S
                steps.link(dve.tensor_tensor(sumA[:, :, 1:E], wT[:, :, 1:E], wT[:, :, 0:E - 1], ALU.add))
                steps.link(dve.tensor_tensor(sumB[:, :, 3:E], sumA[:, :, 3:E], sumA[:, :, 1:E - 2], ALU.add))
                steps.link(dve.tensor_tensor(sumA[:, 1, 7:E], sumB[:, 1, 7:E], sumB[:, 1, 3:E - 4], ALU.add))
                steps.link(dve.tensor_tensor(sumB[:, 1, 15:E], sumA[:, 1, 15:E], sumA[:, 1, 7:E - 8], ALU.add))
                weights_to(U_K + 2, at)
                dve.wait_ge(zuv_ready, at.at(2, 2))
                for t in range(T):
                    n = steps.mark(dve.bn_stats(bn6[:, t, :], zuv[:, t, HC:GN]))
                steps.wait(n)
                dve.sem_inc(passed, 1)
                for t in range(T):
                    n = steps.mark(dve.bn_aggr(bn2[:, t, :], bn6[:, t, :]))
                steps.wait(n)
                dve.tensor_scalar(var[:, V_SGU, :], bn2[:, :, 1], EPS, None, ALU.add).then_inc(var_ready, 1)
                halves = [(sumA, 0), (sumB, 1)]
                for s_, f in halves:
                    rows = slice(64 * f, 64 * f + 64)
                    n = steps.mark(dve.tensor_tensor(s_[rows, :, PAD_D:E], s_[rows, :, PAD_D:E], inv_count[rows, :, :], ALU.mult))
                steps.wait(n)
                for s_, f in halves:
                    rows = slice(64 * f, 64 * f + 64)
                    dve.tensor_tensor(sg[rows, :, :], s_[rows, :, PAD_D:E], wT[rows, :, PAD_D:E], ALU.subtract).then_inc(pooled_ready, 1)
                dve.wait_ge(rstd_ready, at.at(6, 4))
                for t in range(T):
                    dve.tensor_scalar(zuv[:, t, HC:GN], zuv[:, t, HC:GN], bn2[:, t, 0:1], rstd[:, V_SGU, t:t + 1],
                                      ALU.subtract, ALU.mult).then_inc(vhat_ready, 1)
                y_lo(0, 0, y32)
                conv_taps(6)
                weights_to(U_K + 3, at)
                conv_taps(6)
                weights_to(U_V0, at)
                dve.wait_ge(sgu_done, at.at(1, 1))
                dve.wait_ge(pool_done, at.at(1, 1))
                for ct in range(2):
                    o = 5 * KT + ct * ROWS_C + R_SGU
                    for f in range(2):
                        rows = slice(64 * f, 64 * f + 64)
                        mixed = acc[SGU_PAIR][ct][rows, :].rearrange("p (t f s) -> p f t s", t=T, f=2)[:, f, :, :]
                        bias = sgub[rows, bass.ds(l, 1), ct, :].to_broadcast([64, T, P])
                        n = steps.mark(dve.scalar_tensor_tensor(
                            out=sg[rows, ct, :].rearrange("p (t s) -> p t s", t=T), in0=mixed, scalar=par[rows, o:o + 1],
                            in1=bias, op0=ALU.mult, op1=ALU.add))
                steps.wait(n)
                dve.wait_ge(turned, at.at(T_LAYER, T_PRO + T_AT["u"] + 1))
                dve.tensor_tensor(y32, sg, tb[TB["u"]][:, :].rearrange("p (c s) -> p c s", c=2), ALU.mult).then_inc(y32_ready, 1)
                conv_taps(2)
                y_lo(1, 2, y32)
                conv_taps(4)
                y_lo(2, 6, y32)
                conv_taps(6)
                weights_to(U_V0 + 1, at)
                conv_taps(2 * TAPS_C)
                weights_to(U_MO, at)
                dve.wait_ge(turned, at.at(T_LAYER, T_PRO + T_AT["conv"] + 1))
                for t in range(T):
                    n = steps.mark(dve.bn_stats(bn6[:, t, :], tb[TB["conv"]][:, t * W:(t + 1) * W]))
                steps.wait(n)
                dve.sem_inc(passed, 1)
                for t in range(T):
                    n = steps.mark(dve.bn_aggr(bn2[:, t, :], bn6[:, t, :]))
                steps.wait(n)
                dve.tensor_scalar(var[:, V_CLN, :], bn2[:, :, 1], EPS, None, ALU.add).then_inc(var_ready, 1)
                dve.wait_ge(rstd_ready, at.at(6, 5))
                for t in range(T):
                    dve.tensor_scalar(hact[:, t, :], tb[TB["conv"]][:, t * W:(t + 1) * W], bn2[:, t, 0:1],
                                      rstd[:, V_CLN, t:t + 1], ALU.subtract, ALU.mult).then_inc(cnorm_ready, 1)
                weights_to(U_MO + 2, at)
                y_lo(3, 4, y32)
                weights_to(U_MO + 3, at)

                def boundary(u_end, b, g, name, pairs, i_var, factor):
                    weights_to(u_end + 2, at)
                    update(b, 0, 0, u_end, pairs[0], factor, at)
                    update(b, 0, 1, u_end, pairs[0], factor, at)
                    weights_to(u_end + 3, at)
                    gained(b + 1, 0, 0, g, f"{name}00", at)
                    xT_lo_part(b + 1, 0, 0, at)
                    gained(b + 1, 0, 1, g, f"{name}01", at)
                    xT_lo_part(b + 1, 0, 1, at)
                    update(b, 1, 0, u_end + 2, pairs[1], factor, at)
                    weights_to(u_end + 4, at)
                    update(b, 1, 1, u_end + 2, pairs[1], factor, at)
                    gained(b + 1, 1, 0, g, f"{name}10", at)
                    xT_lo_part(b + 1, 1, 0, at)
                    gained(b + 1, 1, 1, g, f"{name}11", at)
                    xT_lo_part(b + 1, 1, 1, at)
                    dve.wait_ge(x_squared, at.at(16, 8 + 4 * (b + 1)))
                    variance(i_var, steps)
                    weights_to(u_end + 5, at)

                boundary(U_MO + 1, 1, G_XATTN, "q_in", MO_PAIR, V_Q, 1.0)

                def softmax_max(h):
                    dve.wait_ge(scores_done, at.at(HEADS, h + 1))
                    steps.link(dve.tensor_reduce(smax[:, h, :], acc[SPAIR[h // 2]][h % 2][:, :].rearrange("p (t s) -> p t s", t=T),
                                                 AX.X, ALU.max))
                    dve.tensor_scalar(nmax[:, h, :], smax[:, h, :], -SCALE, None, ALU.mult).then_inc(nmax_ready, 1)

                def inv_sum(h):
                    dve.wait_ge(probs_ready, at.at(HEADS * T, T * (h + 1)))
                    dve.reciprocal(rinv[:, h, :], psum_rows[:, h, :]).then_inc(rinv_ready, 1)

                def probs_turn(h):
                    dve.wait_ge(turned, at.at(T_LAYER, T_PRO + T_AT[f"p{h}"] + 1))
                    dve.tensor_copy(pT[h], tb[TB[f"p{h}"]][:, :].rearrange("p (k s) -> p k s", k=2)).then_inc(pT_ready, 1)

                def attn_lo(h):
                    rows = slice(Y_KT + 2 * h, Y_KT + 2 * h + 2)
                    dve.wait_ge(oT_hi_ready, at.at(HEADS, h + 1))
                    dve.tensor_tensor(hT_lo[:, rows, :], tb[TB[f"o{h}"]][:, :].rearrange("p (k s) -> p k s", k=2),
                                      hT_hi[:, rows, :].bitcast(F32), ALU.subtract).then_inc(oT_ready, 1)

                weights_to(U_V1 + 1, at)
                softmax_max(0)
                softmax_max(1)
                inv_sum(0)
                inv_sum(1)
                weights_to(U_WO, at)
                softmax_max(2)
                softmax_max(3)
                probs_turn(0)
                probs_turn(1)
                inv_sum(2)
                inv_sum(3)
                probs_turn(2)
                probs_turn(3)
                weights_to(U_WO + 2, at)
                for h in range(HEADS):
                    attn_lo(h)
                boundary(U_WO + 1, 2, G_FFN2, "f2in", WO_PAIR, V_F2, 1.0)
                weights_to(U_F2I + 3, at)
                ffn(l, U_F2I, 1)
                weights_to(U_F2O + 7, at)
                update(3, 0, 0, U_F2O + 5, F2O_PAIR[0], 0.5, at)
                update(3, 0, 1, U_F2O + 5, F2O_PAIR[0], 0.5, at)
                weights_to(U_F2O + 8, at)
                gained(4, 0, 0, G_FFN1, "next00", at, layer=l + 1)
                weights_to(U_F2O + 9, at)
                xT_lo_part(4, 0, 0, at)
                gained(4, 0, 1, G_FFN1, "next01", at, layer=l + 1)
                xT_lo_part(4, 0, 1, at)
                weights_to(UNITS, at)
                update(3, 1, 0, U_F2O + 11, F2O_PAIR[1], 0.5, at)
                weights_to(UNITS + 1, at)
                update(3, 1, 1, U_F2O + 11, F2O_PAIR[1], 0.5, at)
                dve.wait_ge(x_squared, at.at(16, 8 + 16))
                variance(V_X, steps)
                assert steps.n == DVE_STEPS, steps.n

            dve.wait_ge(rstd_ready, 2 + 6 * L)
            dve.wait_ge(gf_landed, 16)
            gf = memT[:, 0:4, :].rearrange("p k s -> p (k s)")
            for t in range(T):
                dve.scalar_tensor_tensor(out=xs[:, t, :], in0=xs[:, t, :], scalar=rstd[:, V_X, t:t + 1], in1=gf,
                                         op0=ALU.mult, op1=ALU.mult).then_inc(final_ready, 1)

        @block.tensor
        def _(pe):
            pe.sem_inc(unit_done, 2 * SLOTS)

            def turn(b, pieces):
                for col, src in pieces:
                    k, m = src.shape[0], src.shape[1]
                    ins = pe.transpose(tb[b][0:m, col:col + k], src, ident[0:k, 0:k])
                ins.then_inc(turned, 1)

            pe.wait_ge(consts_ready, 1)
            pe.wait_ge(rowsg_landed, 16 * 5)
            turn(0, [(10 * k, rows_g[0:10, k * P:(k + 1) * P]) for k in range(KT)])
            pe.wait_ge(x_landed, 16)
            for t in range(T):
                if t:
                    pe.wait_ge(par_ready, 1)
                turn(TB[f"start0{t}"], [(j * P, xs[:, t, j * P:(j + 1) * P]) for j in range(4)])
            pe.wait_ge(rowsc_landed, 16 * 6)
            pe.wait_ge(xg_ready, 1)
            turn(1, [(2 * ROWS_C * c, rows_c[0:2 * ROWS_C, c * P:(c + 1) * P]) for c in range(2)])
            pe.wait_ge(mem_landed, 16)
            for i, (n, t) in enumerate(part):
                if i == 0:
                    pe.wait_ge(xg_ready, 2)
                elif i == 1:
                    pe.wait_ge(par_ready, 2)
                else:
                    pe.wait_ge(memT_ready, i - 1)
                turn(i % 2, [(j * P, mem_sb[:, t, (4 * n + j) * P:(4 * n + j + 1) * P]) for j in range(4)])
            pe.wait_ge(consts_ready, 2)
            for i in range(2):
                pe.wait_ge(memT_ready, 3 + i)
                turn(i, [(h * P, sgu_raw[:, 4 * i + h, :]) for h in range(4)])
            pe.wait_ge(sguT_ready, 2)

            def unit(u, at, pair, s_hi, s_lo, k0, first, last, k=0, before=None, between=None):
                pe.wait_ge(w_split, at.at(UNITS, SLOTS + u + 1, k))
                slot = u % SLOTS
                nk = unit_kt(u)
                for t in range(T):
                    if before:
                        before(t)
                    for j in range(nk):
                        hi = s_hi[:, k0 + j, t * P:(t + 1) * P]
                        lo = s_lo[:, k0 + j, t * P:(t + 1) * P]
                        wh = w_hi[:, slot, j * GN:(j + 1) * GN]
                        wl = w_lo[:, slot, j * GN:(j + 1) * GN]
                        o = acc[pair][t][:, :]
                        pe.matmul(o, hi, wh, start=(first and j == 0), stop=False)
                        pe.matmul(o, hi, wl, start=False, stop=False)
                        ins = pe.matmul(o, lo, wh, start=False, stop=(last and j == nk - 1))
                    ins.then_inc(unit_done, 1)
                    if between:
                        between(t)

            def x_turn(b, n, t, name, at):
                pe.wait_ge(x_updated, at.at(16, T + 4 * (b - 1) + 2 * n + t + 1 if b else t + 1))
                if n:
                    pe.wait_ge(xg_ready, at.at(16, 4 * b + t + 1))
                turn(TB[name], [(j * P, xs[:, t, (4 * n + j) * P:(4 * n + j + 1) * P]) for j in range(4)])

            def xT_wait(b, n, at):
                return lambda t: pe.wait_ge(xT_ready, at.at(16, 4 * b + 2 * n + t + 1))

            def ffn(l, base, f, first_between):
                at0 = Layer(l)
                b = 3 if f else 0

                def hidden_turn(c, at, k=0):
                    pe.wait_ge(hact_ready, at.at(4 * FC, T + 2 * FC * f + 2 * c + 2, 2 * k))
                    pe.wait_ge(hT_ready, at.at(2 * FC, 1 + FC * f + c, k))
                    turn(T_BANK(c), [(kt * S + t * P, hact[:, t, kt * P:(kt + 1) * P]) for kt in range(2) for t in range(T)])

                unit(base, at0, 0, xT_hi, xT_lo, 0, True, False, before=xT_wait(b, 0, at0), between=first_between)
                unit(base + 1, at0, 0, xT_hi, xT_lo, GK, False, True, before=xT_wait(b, 1, at0))
                with pe.Fori(0, 3) as it:
                    at = Layer(l, it)
                    for c in range(1, 4):
                        unit(base + 2 * c, at, c % 3, xT_hi, xT_lo, 0, True, False, k=6)
                        hidden_turn(c - 1, at, 3)
                        unit(base + 2 * c + 1, at, c % 3, xT_hi, xT_lo, GK, False, True, k=6)
                c = FC - 1
                unit(base + 2 * c, at0, c % 3, xT_hi, xT_lo, 0, True, False)
                hidden_turn(c - 1, at0)
                unit(base + 2 * c + 1, at0, c % 3, xT_hi, xT_lo, GK, False, True)
                pairs = F2O_PAIR if f else F1O_PAIR
                for n in range(2):
                    for j in range(NGO):
                        u = base + 2 * FC + n * NGO + j
                        if n == 0:
                            pe.wait_ge(hT_ready, at0.at(2 * FC, 1 + FC * f + min(2 * j + 2, FC)))
                        unit(u, at0, pairs[n], hT_hi, hT_lo, GK * j, j == 0, j == NGO - 1)
                        if n == 0 and j == 0:
                            hidden_turn(FC - 1, at0)
                        if n == 1 and j < 2:
                            x_turn(4 if f else 1, 0, j, f"next0{j}" if f else f"mi0{j}", at0)

            with pe.Fori(0, L) as l:
                at = Layer(l)
                x_turn(0, 1, 0, "start10", at)
                ffn(l, U_F1I, 0, lambda t: None if t else x_turn(0, 1, 1, "start11", at))

                x_turn(1, 1, 0, "mi10", at)
                unit(U_MI, at, 1, xT_hi, xT_lo, 0, True, False, before=xT_wait(1, 0, at),
                     between=lambda t: None if t else x_turn(1, 1, 1, "mi11", at))
                unit(U_MI + 1, at, 1, xT_hi, xT_lo, GK, False, True, before=xT_wait(1, 1, at))
                unit(U_MI + 2, at, 2, xT_hi, xT_lo, 0, True, False)

                def pairs_of(tile, col):
                    return [(ct * S + t * P, tile[:, t, col + ct * P:col + (ct + 1) * P]) for ct in range(2) for t in range(T)]

                pe.wait_ge(glu_ready, at.at(2, 2))
                turn(0, pairs_of(hact, 0))
                unit(U_MI + 3, at, 2, xT_hi, xT_lo, GK, False, True)
                unit(U_MI + 4, at, 0, xT_hi, xT_lo, 0, True, False)
                pe.wait_ge(am_ready, at.at(2, 2))
                turn(1, pairs_of(hact, 0))
                unit(U_MI + 5, at, 0, xT_hi, xT_lo, GK, False, True)
                unit(U_MI + 6, at, 1, xT_hi, xT_lo, 0, True, False)
                pe.wait_ge(zbd_ready, at.at(2, 2))
                pe.wait_ge(gluT_ready, at.at(1, 1))
                turn(TB["b"], pairs_of(zbd, 0))
                unit(U_MI + 7, at, 1, xT_hi, xT_lo, GK, False, True)
                pe.wait_ge(amT_ready, at.at(1, 1))
                turn(TB["w"], pairs_of(zbd, HC))

                def mem_unit(u, pair, k0, first):
                    unit(u, at, pair, hT_hi, hT_lo, MEM_KT + k0, first, not first)

                pe.wait_ge(mT_ready, at.at(4, 2))
                mem_unit(U_K, KPAIR, 0, True)
                pe.wait_ge(mT_ready, at.at(4, 4))
                mem_unit(U_K + 1, KPAIR, GK, False)
                pe.wait_ge(vhat_ready, at.at(2, 2))
                for ct in range(2):
                    for t in range(T):
                        ins = pe.matmul(acc[SGU_PAIR][ct][:, t * S:(t + 1) * S], zuv[:, t, HC + ct * P:HC + (ct + 1) * P],
                                        sguT[:, bass.ds(l, 1), 2 * ct:2 * ct + 2, :].rearrange("p o h t -> p (o h t)"),
                                        start=True, stop=True)
                ins.then_inc(sgu_done, 1)
                pe.wait_ge(pooled_ready, at.at(2, 2))
                for ct in range(2):
                    ins = pe.matmul(acc[POOL_PAIR][ct][:, 0:S], poolw[:, ct, :], sg[:, ct, :], start=True, stop=True)
                ins.then_inc(pool_done, 1)
                pe.wait_ge(y32_ready, at.at(4, 1))
                turn(TB["u"], pairs_of(zuv, 0))
                def key_turns(n, free):
                    for t in range(T):
                        pe.wait_ge(k_ready, at.at(4, 2 * n + t + 1))
                        free(t)
                        turn(TB[f"k{n}{t}"], [(j * P, kbuf[:, t, j * P:(j + 1) * P]) for j in range(4)])

                pe.wait_ge(k_ready, at.at(4, 2))
                mem_unit(U_K + 2, KPAIR, 0, True)
                mem_unit(U_K + 3, KPAIR, GK, False)
                key_turns(0, lambda t: pe.wait_ge(wT_ready, at.at(1, 1)) if TB[f"k0{t}"] == TB["w"]
                          else pe.wait_ge(y32_ready, at.at(4, 2)))
                mem_unit(U_V0, VPAIR[0], 0, True)
                key_turns(1, lambda t: pe.wait_ge(kT_ready, at.at(4, t + 1)))

                def conv_turn(t):
                    if t == 0:
                        pe.wait_ge(conv_ready, at.at(1, 1))
                        pe.wait_ge(kT_ready, at.at(4, 4))
                        turn(TB["conv"], [(t * W + ct * P, cacc[:, ct, t * P:(t + 1) * P]) for t in range(T) for ct in range(2)])

                def norm_turn(t):
                    if t == 0:
                        pe.wait_ge(cnorm_ready, at.at(2, 2))
                        turn(TB["norm"], pairs_of(hact, 0))

                unit(U_V0 + 1, at, VPAIR[0], hT_hi, hT_lo, MEM_KT + GK, False, True, between=conv_turn)

                pe.wait_ge(y_ready, at.at(4, 3))
                unit(U_MO, at, MO_PAIR[0], hT_hi, hT_lo, Y_KT, True, False, between=norm_turn)
                pe.wait_ge(y_ready, at.at(4, 4))
                unit(U_MO + 1, at, MO_PAIR[0], hT_hi, hT_lo, Y_KT + GK, False, True)
                unit(U_MO + 2, at, MO_PAIR[1], hT_hi, hT_lo, Y_KT, True, False,
                     between=lambda t: x_turn(2, 0, t, f"q_in0{t}", at))
                unit(U_MO + 3, at, MO_PAIR[1], hT_hi, hT_lo, Y_KT + GK, False, True)

                pe.wait_ge(v_ready, at.at(4, 2))
                x_turn(2, 1, 0, "q_in10", at)
                unit(U_Q, at, QPAIR[0], xT_hi, xT_lo, 0, True, False, before=xT_wait(2, 0, at),
                     between=lambda t: None if t else x_turn(2, 1, 1, "q_in11", at))
                unit(U_Q + 1, at, QPAIR[0], xT_hi, xT_lo, GK, False, True, before=xT_wait(2, 1, at))

                def query_turn(n, t):
                    pe.wait_ge(q_ready, at.at(4, 2 * n + t + 1))
                    if n:
                        pe.wait_ge(qT_ready, at.at(4, t + 1))
                    turn(TB[f"q{n}{t}"], [(j * P, kq[:, t, j * P:(j + 1) * P]) for j in range(4)])

                unit(U_Q + 2, at, QPAIR[1], xT_hi, xT_lo, 0, True, False)
                query_turn(0, 0)
                query_turn(0, 1)
                unit(U_Q + 3, at, QPAIR[1], xT_hi, xT_lo, GK, False, True)

                def scores(h):
                    for t in range(T):
                        for d in range(2):
                            ins = pe.matmul(acc[SPAIR[h // 2]][h % 2][:, t * S:(t + 1) * S], qT[:, 2 * h + d, t * P:(t + 1) * P],
                                            kT[:, 2 * h + d, :], start=(d == 0), stop=(d == 1))
                    ins.then_inc(scores_done, 1)

                pe.wait_ge(qT_ready, at.at(4, 2))
                scores(0)
                scores(1)
                unit(U_V1, at, VPAIR[1], hT_hi, hT_lo, MEM_KT, True, False, between=lambda t: query_turn(1, t))
                pe.wait_ge(qT_ready, at.at(4, 4))
                scores(2)
                scores(3)

                def probs_turns(h):
                    pe.wait_ge(probs_ready, at.at(HEADS * T, T * (h + 1)))
                    if h >= 2:
                        pe.wait_ge(pT_ready, at.at(HEADS, h - 1))
                    turn(TB[f"p{h}"], [(m * S + t * P, probs[:, T * h + t, m * P:(m + 1) * P]) for m in range(2) for t in range(T)])

                def pv(h):
                    pe.wait_ge(pT_ready, at.at(HEADS, h + 1))
                    for t in range(T):
                        for m in range(2):
                            ins = pe.matmul(acc[OPAIR[h // 2]][h % 2][:, t * S:(t + 1) * S], pT[h][:, m, t * P:(t + 1) * P],
                                            v_half[h // 2][:, m, (h % 2) * HD:(h % 2 + 1) * HD], start=(m == 0), stop=(m == 1))
                    ins.then_inc(pv_done, 1)

                def attn_turns(h):
                    pe.wait_ge(attn_ready, at.at(HEADS, h + 1))
                    if h >= 2:
                        pe.wait_ge(oT_ready, at.at(HEADS, h - 1))
                    else:
                        pe.wait_ge(pT_ready, at.at(HEADS, h + 3))
                    turn(TB[f"o{h}"], [(d * S + t * P, attn[h % 2][:, t, d * P:(d + 1) * P]) for d in range(2) for t in range(T)])

                probs_turns(0)
                probs_turns(1)
                mem_unit(U_V1 + 1, VPAIR[1], GK, False)
                probs_turns(2)
                pe.wait_ge(v_ready, at.at(4, 2))
                pv(0)
                probs_turns(3)
                pv(1)
                attn_turns(0)
                pe.wait_ge(v_ready, at.at(4, 4))
                pv(2)
                attn_turns(1)
                pv(3)
                attn_turns(2)
                pe.wait_ge(oT_ready, at.at(HEADS, 2))
                unit(U_WO, at, WO_PAIR[0], hT_hi, hT_lo, Y_KT, True, False, between=lambda t: None if t else attn_turns(3))
                pe.wait_ge(oT_ready, at.at(HEADS, 4))
                unit(U_WO + 1, at, WO_PAIR[0], hT_hi, hT_lo, Y_KT + GK, False, True)
                unit(U_WO + 2, at, WO_PAIR[1], hT_hi, hT_lo, Y_KT, True, False,
                     between=lambda t: x_turn(3, 0, t, f"f2in0{t}", at))
                unit(U_WO + 3, at, WO_PAIR[1], hT_hi, hT_lo, Y_KT + GK, False, True)
                x_turn(3, 1, 0, "f2in10", at)
                ffn(l, U_F2I, 1, lambda t: None if t else x_turn(3, 1, 1, "f2in11", at))


_INS = ["x", "mem", "norm_ffn1", "ffn1_w_in", "ffn1_w_out", "norm_mix", "mix_w_in", "sconv_w", "sgu_norm_g", "sgu_w", "sgu_b",
        "cconv_w", "cconv_ln_g", "cconv_ln_b", "pool_w", "pool_scale", "mix_w_out", "norm_xattn", "norm_mem", "xattn_wq",
        "xattn_wkv", "xattn_wo", "norm_ffn2", "ffn2_w_in", "ffn2_w_out", "norm_final"]


def kernel(**inputs):
    import numpy as np
    import concourse.bacc as bacc
    from concourse.bass_utils import run_bass_kernel_spmd

    nc = bacc.Bacc("TRN2", target_bir_lowering=False, num_devices=1)
    arrays, args = {}, []
    for name in _INS:
        a = np.ascontiguousarray(inputs[name])
        arrays[f"in_{name}"] = a
        args.append(nc.dram_tensor(f"in_{name}", a.shape, mybir.dt.from_np(a.dtype), kind="ExternalInput").ap())
    out = nc.dram_tensor("out_0", inputs["x"].shape, F32, kind="ExternalOutput").ap()
    trunk_kernel(nc, *args, out)
    r = run_bass_kernel_spmd(nc, [arrays], core_ids=[0])
    return r.results[0]["out_0"]
```
